# Optimizing a Trainium2 kernel written in Bass

```python
import jax, jax.numpy as jnp
from jax import lax
import numpy as np

D_MODEL = 2048
BATCH = 1
SEQ = 256
DEPTH = 2

CHUNK = 64
RMS_EPS = 1e-6

A_HEAD_DIM = 64
A_HEADS = (D_MODEL // 2) // A_HEAD_DIM
A_KV_HEADS = A_HEADS // 4
A_Q_PER_KV = A_HEADS // A_KV_HEADS
A_WIDTH = A_HEADS * A_HEAD_DIM
A_KV_WIDTH = A_KV_HEADS * A_HEAD_DIM
WINDOW = 128
WIN_CHUNKS = WINDOW // CHUNK
BAND = WIN_CHUNKS * CHUNK

GMLP_BLOCK = 128
B_GROUP_DIM = 128
B_GROUPS = (D_MODEL // 2) // B_GROUP_DIM
B_WIDTH = B_GROUPS * B_GROUP_DIM

HYB_IN_WIDTH = A_WIDTH + 2 * A_KV_WIDTH + 2 * B_WIDTH
HYB_MIX_WIDTH = A_WIDTH + B_WIDTH

C_HEAD_DIM = 128
C_HEADS = D_MODEL // C_HEAD_DIM
C_WIDTH = C_HEADS * C_HEAD_DIM
SB_QBLOCK = 128

FFN_HIDDEN = ((8 * D_MODEL // 3 + 255) // 256) * 256

N_EVEN = (DEPTH + 1) // 2
N_ODD = DEPTH // 2

kernel_name = "hybrid_swa_gmlp_stickbreaking_encoder"

def rms_norm(x, w):
    xf = x.astype(jnp.float32)
    y = xf * lax.rsqrt(jnp.mean(xf * xf, axis=-1, keepdims=True) + RMS_EPS)
    return (y * w.astype(jnp.float32)).astype(x.dtype)

def alibi_slopes(n_heads):
    return jnp.asarray(2.0 ** (-8.0 * np.arange(1, n_heads + 1) / n_heads), dtype=jnp.float32)

def sliding_window_sink_attention(q, k, v, q_norm_w, k_norm_w, sinks):
    b, s = q.shape[0], q.shape[1]
    nc = s // CHUNK
    qf = rms_norm(q, q_norm_w).astype(jnp.float32) * (A_HEAD_DIM ** -0.5)
    kf = rms_norm(k, k_norm_w).astype(jnp.float32)
    vf = v.astype(jnp.float32)
    qc = qf.reshape(b, nc, CHUNK, A_KV_HEADS, A_Q_PER_KV, A_HEAD_DIM)

    def band(t):
        tc = t.reshape(b, nc, CHUNK, A_KV_HEADS, A_HEAD_DIM)
        tp = jnp.pad(tc, ((0, 0), (WIN_CHUNKS - 1, 0), (0, 0), (0, 0), (0, 0)))
        return jnp.concatenate([tp[:, o:o + nc] for o in range(WIN_CHUNKS)], axis=2)

    kb, vb = band(kf), band(vf)
    logits = jnp.einsum('bnqhgd,bnkhd->bnhgqk', qc, kb)
    qi = jnp.arange(CHUNK)
    ki = jnp.arange(BAND)
    dist = jnp.abs(qi[:, None] - ki[None, :] + (WIN_CHUNKS - 1) * CHUNK).astype(jnp.float32)
    slopes = alibi_slopes(A_HEADS).reshape(A_KV_HEADS, A_Q_PER_KV, 1, 1)
    key_pos = (jnp.arange(nc)[:, None] - (WIN_CHUNKS - 1)) * CHUNK + ki[None, :]
    valid = (key_pos >= 0)[:, None, None, None, :]
    logits = jnp.where(valid, logits - slopes * dist, -jnp.inf)
    sink = sinks.astype(jnp.float32).reshape(A_KV_HEADS, A_Q_PER_KV, 1, 1)
    m = jnp.maximum(jnp.max(logits, axis=-1, keepdims=True), sink)
    p = jnp.exp(logits - m)
    probs = p / (jnp.sum(p, axis=-1, keepdims=True) + jnp.exp(sink - m))
    o = jnp.einsum('bnhgqk,bnkhd->bnqhgd', probs, vb)
    return o.reshape(b, s, A_WIDTH)

def spatial_gating(u, g, gate_norm_w, w_spatial, b_spatial):
    b, s = u.shape[0], u.shape[1]
    nb = s // GMLP_BLOCK
    u = jax.nn.gelu(u).reshape(b, nb, GMLP_BLOCK, B_GROUPS, B_GROUP_DIM)
    g = rms_norm(jax.nn.gelu(g).reshape(b, s, B_GROUPS, B_GROUP_DIM), gate_norm_w)
    g = g.reshape(b, nb, GMLP_BLOCK, B_GROUPS, B_GROUP_DIM)
    idx = jnp.arange(GMLP_BLOCK) // CHUNK
    chunk_causal = idx[None, :] <= idx[:, None]
    ws = jnp.where(chunk_causal[None], w_spatial, 0.0).astype(g.dtype)
    gate = jnp.einsum('gij,bnjgc->bnigc', ws, g) + b_spatial.T.astype(g.dtype)[:, :, None]
    return (u * gate).reshape(b, s, B_WIDTH)

def stick_breaking_attention(q, k, v):
    b, s = q.shape[0], q.shape[1]
    qf = q.astype(jnp.float32) * (C_HEAD_DIM ** -0.5)
    kf = k.astype(jnp.float32)
    vf = v.astype(jnp.float32)
    outs = []
    for i in range(s // SB_QBLOCK):
        q0, q1 = i * SB_QBLOCK, (i + 1) * SB_QBLOCK
        z = jnp.einsum('bqhd,bkhd->bhqk', qf[:, q0:q1], kf[:, :q1])
        mask = (q0 + jnp.arange(SB_QBLOCK))[:, None] > jnp.arange(q1)[None, :]
        log_beta = jax.nn.log_sigmoid(z)
        log_keep = jnp.where(mask, jax.nn.log_sigmoid(-z), 0.0)
        later = lax.cumsum(log_keep, axis=3, reverse=True) - log_keep
        w = jnp.where(mask, jnp.exp(log_beta + later), 0.0)
        outs.append(jnp.einsum('bhqk,bkhd->bqhd', w, vf[:, :q1]))
    return jnp.concatenate(outs, axis=1).reshape(b, s, C_WIDTH)

def swiglu(h, w_gate, w_up, w_down):
    return (jax.nn.silu(h @ w_gate) * (h @ w_up)) @ w_down

def setup_inputs(seed: int = 0) -> dict:
    key = jax.random.key(seed)
    ks = jax.random.split(key, 20)
    nrm = lambda k, shape, scale: jax.random.normal(k, shape, jnp.float32) * scale
    return {
        "x": nrm(ks[0], (BATCH, SEQ, D_MODEL), 1.0),
        "mixer_norm_w": 1.0 + nrm(ks[1], (DEPTH, D_MODEL), 0.02),
        "ffn_norm_w": 1.0 + nrm(ks[2], (DEPTH, D_MODEL), 0.02),
        "w_ffn_gate": nrm(ks[3], (DEPTH, D_MODEL, FFN_HIDDEN), D_MODEL ** -0.5),
        "w_ffn_up": nrm(ks[4], (DEPTH, D_MODEL, FFN_HIDDEN), D_MODEL ** -0.5),
        "w_ffn_down": nrm(ks[5], (DEPTH, FFN_HIDDEN, D_MODEL), FFN_HIDDEN ** -0.5),
        "hyb_w_in": nrm(ks[6], (N_EVEN, D_MODEL, HYB_IN_WIDTH), D_MODEL ** -0.5),
        "hyb_q_norm_w": 1.0 + nrm(ks[7], (N_EVEN, A_HEAD_DIM), 0.02),
        "hyb_k_norm_w": 1.0 + nrm(ks[8], (N_EVEN, A_HEAD_DIM), 0.02),
        "hyb_sinks": nrm(ks[9], (N_EVEN, A_HEADS), 0.5),
        "hyb_gate_norm_w": 1.0 + nrm(ks[10], (N_EVEN, B_GROUPS, B_GROUP_DIM), 0.02),
        "hyb_w_spatial": nrm(ks[11], (N_EVEN, B_GROUPS, GMLP_BLOCK, GMLP_BLOCK), GMLP_BLOCK ** -0.5),
        "hyb_b_spatial": 1.0 + nrm(ks[12], (N_EVEN, B_GROUPS, GMLP_BLOCK), 0.02),
        "hyb_w_out": nrm(ks[13], (N_EVEN, HYB_MIX_WIDTH, D_MODEL), HYB_MIX_WIDTH ** -0.5),
        "sb_w_qkv": nrm(ks[14], (N_ODD, D_MODEL, 3 * C_WIDTH), D_MODEL ** -0.5),
        "sb_w_out": nrm(ks[15], (N_ODD, C_WIDTH, D_MODEL), C_WIDTH ** -0.5),
    }

def reference(x, mixer_norm_w, ffn_norm_w, w_ffn_gate, w_ffn_up, w_ffn_down,
              hyb_w_in, hyb_q_norm_w, hyb_k_norm_w, hyb_sinks, hyb_gate_norm_w,
              hyb_w_spatial, hyb_b_spatial, hyb_w_out, sb_w_qkv, sb_w_out):
    b, s, _ = x.shape
    a_split = [A_WIDTH, A_WIDTH + A_KV_WIDTH, A_WIDTH + 2 * A_KV_WIDTH,
               A_WIDTH + 2 * A_KV_WIDTH + B_WIDTH]
    for layer in range(DEPTH):
        j = layer // 2
        h = rms_norm(x, mixer_norm_w[layer])
        if layer % 2 == 0:
            proj = h @ hyb_w_in[j]
            q, k, v, u, g = jnp.split(proj, a_split, axis=-1)
            q = q.reshape(b, s, A_HEADS, A_HEAD_DIM)
            k = k.reshape(b, s, A_KV_HEADS, A_HEAD_DIM)
            v = v.reshape(b, s, A_KV_HEADS, A_HEAD_DIM)
            attn = sliding_window_sink_attention(q, k, v, hyb_q_norm_w[j], hyb_k_norm_w[j], hyb_sinks[j])
            sgu = spatial_gating(u, g, hyb_gate_norm_w[j], hyb_w_spatial[j], hyb_b_spatial[j])
            mixed = jnp.concatenate([attn.astype(x.dtype), sgu.astype(x.dtype)], axis=-1) @ hyb_w_out[j]
        else:
            qkv = (h @ sb_w_qkv[j]).reshape(b, s, 3, C_HEADS, C_HEAD_DIM)
            o = stick_breaking_attention(qkv[:, :, 0], qkv[:, :, 1], qkv[:, :, 2])
            mixed = o.astype(x.dtype) @ sb_w_out[j]
        x = x + mixed
        h = rms_norm(x, ffn_norm_w[layer])
        x = x + swiglu(h, w_ffn_gate[layer], w_ffn_up[layer], w_ffn_down[layer])
    return x


_drawn_inputs = setup_inputs


def setup_inputs(seed=0):
    import zlib

    import numpy as np

    out = dict(_drawn_inputs(seed))
    spreads = {}
    factors = {'mixer_norm_w': 2.754,
     'ffn_norm_w': 3.141,
     'hyb_q_norm_w': 8.0,
     'hyb_k_norm_w': 8.0,
     'hyb_sinks': 7.168,
     'hyb_gate_norm_w': 7.041,
     'hyb_b_spatial': 6.128}
    for name, (base, spread) in spreads.items():
        noise = np.random.default_rng([zlib.crc32(name.encode()), seed]).standard_normal(out[name].shape)
        drawn = base * np.exp(spread * noise) if base else spread * noise
        out[name] = __import__('jax').numpy.asarray(drawn.astype(out[name].dtype))
    for name, factor in factors.items():
        out[name] = (out[name] * factor).astype(out[name].dtype)
    return out
```

```python
from contextlib import ExitStack

import numpy as np

import concourse.bass as bass
import concourse.mybir as mybir
from concourse.alu_op_type import AluOpType as ALU

F32 = mybir.dt.float32
F32R = mybir.dt.float32r
ACTF = mybir.ActivationFunctionType
AX = mybir.AxisListType

P = 128
SEQ = 256
D = 2048
TT = SEQ // P
KT = D // P
CH = 512
FFN = 5632
FK = FFN // P
EPS = 1e-6

A_DIM, A_HEADS, A_KV = 64, 16, 4
A_PER = A_HEADS // A_KV
A_W, A_KVW = A_HEADS * A_DIM, A_KV * A_DIM
CHUNK = 64
B_GROUPS, B_DIM = 8, 128
B_W = B_GROUPS * B_DIM
C_DIM, C_HEADS = 128, 16
GRP = CH // P
IN_W = A_W + 2 * A_KVW + 2 * B_W

FULL = [4] * (KT // 4)
DOWN = [4] * 10 + [2, 2]
PHASES = [
    ("in", 1, 7, FULL), ("out", 4, 1, FULL), ("up", FFN // CH, 2, FULL), ("down", D // CH, 1, DOWN),
    ("qkv", 4, 3, FULL), ("out", 4, 1, FULL), ("up", FFN // CH, 2, FULL), ("down", D // CH, 1, DOWN),
]
RING = 4


class Phase:

    def __init__(self, n, unit0, chunk0, turn0):
        self.name, self.count, self.chunks, self.unit_tiles = PHASES[n]
        self.layer = 0 if n < 4 else 1
        self.units = self.chunks * len(self.unit_tiles)
        self.slots = 2 * self.units
        self.per_chunk = 2 * len(self.unit_tiles)
        self.unit0, self.half0, self.chunk0, self.turn0 = unit0, 2 * unit0, chunk0, turn0
        self.turns = {"in": 23, "out": 1, "up": 1, "down": 1 if n < 7 else 0, "qkv": 4}[self.name]

    def half(self, i, s):
        return self.half0 + i * self.slots + s

    def chunk(self, i, c):
        return self.chunk0 + i * self.chunks + c

    def last_half(self, i, c):
        return self.half(i, (c + 1) * self.per_chunk - 1)

    def turn(self, i, k=0):
        return self.turn0 + i * self.turns + k

    def tiles(self, s):
        q = s % self.per_chunk
        n = self.unit_tiles[q // 2] // 2
        return sum(self.unit_tiles[: q // 2]) + (q % 2) * n, n


def make_phases():
    out, unit0, chunk0, turn0 = [], 0, 0, 0
    for n in range(len(PHASES)):
        ph = Phase(n, unit0, chunk0, turn0)
        out.append(ph)
        unit0 += ph.count * ph.units
        if ph.name not in ("out", "down"):
            chunk0 += ph.count * ph.chunks
        turn0 += ph.count * ph.turns
    return out


PH = make_phases()

BLOCKS = 2 * A_KV
BLOCK0 = 22
IN_END = PH[0].slots


def block_start(n):
    return BLOCK0 + 4 * n


IN_TURNS = sorted(
    [(12, "k"), (21, "q0"), (29, "q1"), (44, "gate0"), (48, "mix0"), (IN_END, "gate1"), (IN_END + 4, "mix1")]
    + [(block_start(n) + 4, f"p{n}") for n in range(BLOCKS)]
    + [(block_start(n) + 5, f"o{n}") for n in range(BLOCKS)]
)
IN_TURN = {name: k for k, (_, name) in enumerate(IN_TURNS)}
ROOT = {name: n for n, name in enumerate(["x", "k", "q0", "q1", "g0", "g1", "ffn0", "mix1", "ffn1"])}
SLOPES = [float(np.float32(2.0 ** (-8.0 * (h + 1) / A_HEADS))) for h in range(A_HEADS)]



def roots_per(name):
    return {"x": TT, "k": TT * A_KV, "q0": TT * 8, "q1": TT * 8, "g0": TT * GRP, "g1": TT * GRP}.get(name, TT)


def tails(n, i, first, s, ahead):
    ph, t = PH[n], s - ahead
    out = []
    if not first:
        out.append((ph, i - 1, t + ph.slots))
    elif n:
        out.append((PH[n - 1], PH[n - 1].count - 1, t + PH[n - 1].slots))
    if t >= 0:
        out.append((ph, i, t))
    return out


RESIDUAL = {1: (0, 1, "ffn0"), 3: (1, 2, "mix1"), 5: (2, 3, "ffn1"), 7: (3, None, None)}


def diagonal(ap):
    return ap.rearrange("p (b k) -> p b k", b=3)[:, 0:3:2, :]


def build(nc, x, xT, normw, w_gate, w_up, w_down, w_in, qkw, sinks, gnw, ws, bs, w_out0, w_qkv, w_out1,
          ident, dist, tri, strict, out):
    es = ExitStack()
    with es:
        def sem(name):
            return es.enter_context(nc.semaphore(name))

        def sb(name, shape, dt=F32, ctx=None):
            return (ctx or es).enter_context(nc.sbuf_tensor(name, shape, dt))

        x_sb = sb("x_sb", [P, TT, D])
        xT_hi = sb("xT_hi", [P, KT, SEQ], F32R)
        xT_lo = sb("xT_lo", [P, KT, SEQ], F32R)
        raw = sb("raw", [P, RING, 4, CH])
        w_hi = sb("w_hi", [P, RING, 2, CH], F32R)
        w_lo = sb("w_lo", [P, RING, 2, CH], F32R)
        ident_sb = sb("ident_sb", [P, P])
        tri_sb = sb("tri_sb", [P, P])
        ones_sb = sb("ones_sb", [P, P])
        strict_sb = sb("strict_sb", [P, P])
        normw_sb = sb("normw_sb", [P, 4, KT])
        sinks_sb = sb("sinks_sb", [P, A_HEADS])
        bs_sb = sb("bs_sb", [P, B_GROUPS])
        qkw_sb = sb("qkw_sb", [P, 3])
        squares = sb("squares", [P, TT, 4])
        var = sb("var", [P, 16])
        log = sb("log", [P, 16])
        root = sb("root", [P, 16])
        step = sb("step", [P, 16])
        rstd = sb("rstd", [P, TT])
        top = sb("top", [P, A_PER])
        neg_top = sb("neg_top", [P, A_PER])
        sink_e = sb("sink_e", [P, A_PER])
        sums = sb("sums", [P, A_PER])
        inv = sb("inv", [P, A_PER])

        with ExitStack() as c0:
            m0_hi = sb("m0_hi", [P, KT, SEQ], F32R, c0)
            m0_lo = sb("m0_lo", [P, KT, SEQ], F32R, c0)
            kv = sb("kv", [P, TT, CH], F32, c0)
            k2 = sb("k2", [P, TT, A_KV, 2, A_DIM], F32, c0)
            v2 = sb("v2", [P, TT, A_KV, 2, A_DIM], F32, c0)
            kT = sb("kT", [P, A_KV, SEQ], F32, c0)
            qT = sb("qT", [P, A_HEADS // 2, SEQ], F32, c0)
            qs = kv
            sq = sb("sq", [P, TT, CH], F32, c0)
            wsT = sb("wsT", [P, B_GROUPS, P], F32, c0)
            gnw_sb = sb("gnw_sb", [P, B_W], F32, c0)
            dist_sb = sb("dist_sb", [P, 3 * P], F32, c0)
            with ExitStack() as c1:
                xT_raw = sb("xT_raw", [P, KT, SEQ], F32, c1)
            att = sb("att", [P, 2, A_PER * SEQ], F32, c0)
            gs = sb("gs", [P, TT, CH], F32, c0)
            us = sb("us", [P, TT, CH], F32, c0)
            pT = sb("pT", [P, 2, CH], F32, c0)
        with ExitStack() as c2:
            hT_hi = sb("hT_hi", [P, FK, SEQ], F32R, c2)
            hT_lo = sb("hT_lo", [P, FK, SEQ], F32R, c2)
            hid = sb("hid", [P, TT, CH], F32, c2)
        with ExitStack() as c3:
            m1_hi = sb("m1_hi", [P, KT, SEQ], F32R, c3)
            m1_lo = sb("m1_lo", [P, KT, SEQ], F32R, c3)
            qk1 = sb("qk1", [P, TT, CH], F32, c3)
            v1 = sb("v1", [P, TT, CH], F32, c3)
            qT1 = sb("qT1", [P, GRP, SEQ], F32, c3)
            kT1 = sb("kT1", [P, GRP, SEQ], F32, c3)
            zs = sb("zs", [P, 2, 2, 3 * P], F32, c3)
            soft = sb("soft", [P, 2, 2, 3 * P], F32, c3)
            work = sb("work", [P, 2, 2, 3 * P], F32, c3)

        acc = es.enter_context(nc.psum_tensor("acc", [P, 2, TT, CH], F32))
        turn = es.enter_context(nc.psum_tensor("turn", [P, 2 * CH], F32))
        zb = es.enter_context(nc.psum_tensor("zb", [P, 2 * CH], F32))

        xt_landed = [sem(f"xt_landed{q}") for q in range(4)]
        nw_landed = sem("nw_landed")
        x_landed = sem("x_landed")
        small_landed = sem("small_landed")
        cleared = sem("cleared")
        raw_landed = [sem(f"raw_landed{q}") for q in range(RING)]
        xt_hi = sem("xt_hi")
        xt_lo = sem("xt_lo")
        hi_ready = sem("hi_ready")
        lo_ready = sem("lo_ready")
        products_done = sem("products_done")
        acc_read = sem("acc_read")
        turned = sem("turned")
        act_took = sem("act_took")
        dve_took = sem("dve_took")
        x_added = sem("x_added")
        kept = sem("kept")
        squared = sem("squared")
        root_var, root_log, root_y = sem("root_var"), sem("root_log"), sem("root_y")
        dve_chain = sem("dve_chain")
        scale_ready = sem("scale_ready")
        a_squared = sem("a_squared")
        k_ready, v_ready, q_ready = sem("k_ready"), sem("v_ready"), sem("q_ready")
        logits_done, logits_read = sem("logits_done"), sem("logits_read")
        top_ready, exp_done, p_ready = sem("top_ready"), sem("exp_done"), sem("p_ready")
        g_gelu, g_ready = sem("g_gelu"), sem("g_ready")
        u_gelu, mix_ready = sem("u_gelu"), sem("mix_ready")
        silu_done = sem("silu_done")
        z_done, z_copied, z_abs, z_exp, z_log = (sem(n) for n in ("z_done", "z_copied", "z_abs", "z_exp", "z_log"))
        soft_made, soft_ready, sum_done, diff_ready = (sem(n) for n in ("soft_made", "soft_ready", "sum_done", "diff_ready"))
        w_exp, w_ready = sem("w_exp"), sem("w_ready")
        stored = sem("stored")

        SMALL = [(ident_sb[:], ident), (tri_sb[:], tri), (strict_sb[:], strict), (dist_sb[:], dist),
                 (sinks_sb[:], sinks), (bs_sb[:], bs), (qkw_sb[:, 0:2], qkw), (gnw_sb[:], gnw),
                 (wsT[0:CHUNK], ws[0:CHUNK]), (wsT[CHUNK:P, :, CHUNK:P], ws[CHUNK:P, :, CHUNK:P])]

        def f32(ap):
            return ap.bitcast(F32)

        def lhs(ph):
            if ph.name == "out":
                return (m0_hi, m0_lo) if ph.layer == 0 else (m1_hi, m1_lo)
            return (hT_hi, hT_lo) if ph.name == "down" else (xT_hi, xT_lo)

        def fresh(ph):
            return hid if ph.name == "down" else (kv, qk1)[ph.layer]

        u_col, g_col = A_W + 2 * A_KVW, A_W + 2 * A_KVW + B_W
        IN_COLS = [A_W, 0, CH, g_col, u_col, g_col + CH, u_col + CH]

        def weights(ph, i, c):
            if ph.name == "in":
                return w_in, IN_COLS[c]
            if ph.name == "out":
                return (w_out0, w_out1)[ph.layer], i * CH
            if ph.name == "up":
                return (w_gate, w_up)[c][ph.layer], i * CH
            if ph.name == "down":
                return w_down[ph.layer], i * CH
            return w_qkv, i * CH + c * C_HEADS * C_DIM

        def acc_pair(ph, c):
            return c % 2

        block = es.enter_context(nc.Block())

        @block.sync
        def _(sp):
            for n, ph in enumerate(PH):
                def unit(i, u):
                    c, k = u // len(ph.unit_tiles), u % len(ph.unit_tiles)
                    nk, k0 = ph.unit_tiles[k], sum(ph.unit_tiles[:k])
                    w, col = weights(ph, i, c)
                    src = w.rearrange("(k p) n -> p k n", p=P)[:, k0:k0 + nk, bass.ds(col, CH)]
                    if n or u >= RING:
                        sp.wait_ge(lo_ready, 2 * (ph.unit0 + i * ph.units + u - RING) + 2)
                    sp.dma_start(raw[:, u % RING, 0:nk, :], src).then_inc(raw_landed[u % RING], 16)

                for u in range(ph.units):
                    if n == 0 and u < 4:
                        sp.dma_start(xT_raw[:, 4 * u:4 * u + 4, :], xT[:, 4 * u:4 * u + 4, :]).then_inc(xt_landed[u], 16)
                    unit(0, u)
                if ph.count > 1:
                    with sp.Fori(1, ph.count) as i:
                        for u in range(ph.units):
                            unit(i, u)

        @block.gpsimd
        def _(pool):
            nc.gpsimd.memset(wsT[CHUNK:P, :, 0:CHUNK], 0.0).then_inc(cleared, 1)
            pool.wait_ge(cleared, 1)
            nc.gpsimd.memset(ones_sb[:], 1.0).then_inc(cleared, 1)
            for dst, src in SMALL:
                pool.dma_start(dst, src).then_inc(small_landed, 16)
            last = PH[-1]
            base = 2 * D // CH * 3

            def store(i):
                pool.wait_ge(x_added, base + 2 * i + 2)
                pool.dma_start(out.rearrange("(t p) d -> p t d", p=P)[:, :, bass.ds(i * CH, CH)],
                               x_sb[:, :, bass.ds(i * CH, CH)]).then_inc(stored, 16)

            for i in range(last.count):
                store(i)
            pool.wait_ge(stored, 16 * last.count)

        @block.scalar
        def _(act):
            act.dma_start(normw_sb[:], normw).then_inc(nw_landed, 16)
            act.dma_start(x_sb[:], x.rearrange("(t p) d -> p t d", p=P)).then_inc(x_landed, 16)

            def half(ph, i, s):
                if ph is PH[0] and s < 8 and s % 2 == 0:
                    q = s // 2
                    act.wait_ge(xt_landed[q], 16)
                    if q == 0:
                        act.wait_ge(nw_landed, 16)
                    for k in range(4 * q, 4 * q + 4):
                        ins = nc.scalar.activation(xT_hi[:, k, :], xT_raw[:, k, :], ACTF.Copy, scale=normw_sb[:, 0, k:k + 1])
                    ins.then_inc(xt_hi, 1)
                u = s // 2
                _, nk = ph.tiles(s)
                if s % 2 == 0:
                    act.wait_ge(raw_landed[u % RING], 16 * (ph.unit0 // RING + i * (ph.units // RING) + u // RING + 1))
                if ph is not PH[0] or s >= RING:
                    act.wait_ge(products_done, 2 * (ph.half(i, s) - RING) + 2)
                k = (s % 2) * nk
                nc.scalar.activation(w_hi[:, s % RING, 0:nk, :], raw[:, u % RING, k:k + nk, :], ACTF.Copy).then_inc(hi_ready, 1)

            def take_hi(K, dst, src, scale=None):
                act.wait_ge(turned, K + 1)
                for n, (d, s) in enumerate(zip(dst, src)):
                    if scale is None:
                        ins = nc.scalar.activation(d, s, ACTF.Copy)
                    else:
                        ins = nc.scalar.activation(d, s, ACTF.Copy, scale=scale[n])
                ins.then_inc(act_took, 1)

            def take_root(name):
                r, n = ROOT[name], roots_per(name)
                act.wait_ge(root_var, r + 1)
                nc.scalar.activation(log[:, 0:n], var[:, 0:n], ACTF.Ln).then_inc(root_log, 1)
                act.wait_ge(root_log, r + 1)
                nc.scalar.activation(root[:, 0:n], log[:, 0:n], ACTF.Exp, scale=-0.5).then_inc(root_y, 1)

            def residual(ph, i, t):
                before, row, name = RESIDUAL[PH.index(ph)]
                if row is None:
                    return
                if t == ph.slots:
                    for tt in range(TT):
                        act.wait_ge(x_added, 2 * (before * (D // CH) + i) + tt + 1)
                        nc.scalar.activation(zb[:, tt * CH:(tt + 1) * CH], fresh(ph)[:, tt, :], ACTF.Square,
                                             accum_out=squares[:, tt, bass.ds(i, 1)]).then_inc(squared, 1)
                if t == ph.slots + 1:
                    take_hi(ph.turn(i), [xT_hi[:, bass.ds(i * 4 + k, 1), :] for k in range(4)],
                            [turn[:, k * SEQ:(k + 1) * SEQ] for k in range(4)],
                            [normw_sb[:, row, bass.ds(i * 4 + k, 1)] for k in range(4)])
                if t == ph.slots + 2:
                    nc.scalar.activation(x_sb[:, :, bass.ds(i * CH, CH)], fresh(ph)[:, :, :], ACTF.Copy).then_inc(kept, 1)
                    if isinstance(i, int) and i == ph.count - 1:
                        take_root(name)

            def in_work(t):
                ph = PH[0]
                if t in (2, 3):
                    if t == 2:
                        act.wait_ge(x_landed, 16)
                    else:
                        act.wait_ge(squared, 1)
                    nc.scalar.activation(qT[:, :, :].rearrange("p h t -> p (h t)"), x_sb[:, t - 2, :], ACTF.Square,
                                         accum_out=squares[:, t - 2, 0:1]).then_inc(squared, 1)
                if t == 4:
                    take_root("x")
                if t == 9:
                    act.wait_ge(acc_read, 2)
                    nc.scalar.activation(sq[:, :, 0:A_KVW], kv[:, :, 0:A_KVW], ACTF.Square).then_inc(a_squared, 1)
                    take_root("k")
                if t == 10:
                    for tt in range(TT):
                        src = kv[:, tt, A_KVW:].rearrange("p (h o d) -> p h o d", h=A_KV, o=1)
                        for o in range(2):
                            ins = nc.scalar.activation(v2[:, tt, :, o, :], src[:, :, 0, :], ACTF.Copy)
                    ins.then_inc(v_ready, 1)
                if t == 12:
                    take_hi(ph.turn(0, IN_TURN["k"]), [kT[:, 0:2, :].rearrange("p h t -> p (h t)")], [turn[:, 0:CH]], [qkw_sb[:, 1:2]])
                for b in range(2):
                    if t == 17 + 8 * b:
                        act.wait_ge(acc_read, 2 * (b + 1) + 2)
                        nc.scalar.activation(sq[:, :, :], qs[:, :, :], ACTF.Square).then_inc(a_squared, 1)
                    if t == 18 + 8 * b:
                        take_root(f"q{b}")
                    if t == 21 + 8 * b:
                        act.wait_ge(scale_ready, 1)
                        take_hi(ph.turn(0, IN_TURN[f"q{b}"]), [qT[:, 4 * b:4 * b + 2, :].rearrange("p h t -> p (h t)")],
                                [turn[:, 0:CH]], [qkw_sb[:, 2:3]])
                for b in range(2):
                    o = 16 * b
                    if t == 33 + o:
                        act.wait_ge(acc_read, 2 * (3 + 2 * b) + 2)
                        nc.scalar.activation(gs[:, :, :], gs[:, :, :], ACTF.Gelu_apprx_tanh).then_inc(g_gelu, 1)
                    if t == 34 + o:
                        act.wait_ge(g_gelu, b + 1)
                        nc.scalar.activation(sq[:, :, :], gs[:, :, :], ACTF.Square).then_inc(a_squared, 1)
                    if t == 35 + o:
                        take_root(f"g{b}")
                    if t == 41 + o:
                        act.wait_ge(acc_read, 2 * (4 + 2 * b) + 2)
                        nc.scalar.activation(us[:, :, :], us[:, :, :], ACTF.Gelu_apprx_tanh).then_inc(u_gelu, 1)
                    if t == (44, 58)[b]:
                        K = ph.turn(0, IN_TURN[f"gate{b}"])
                        act.wait_ge(turned, K + 1)
                        for g in range(GRP):
                            ins = nc.scalar.activation(sq[:, 1, g * P:(g + 1) * P], turn[:, CH + g * P:CH + (g + 1) * P],
                                                       ACTF.Identity, bias=bs_sb[:, GRP * b + g:GRP * b + g + 1])
                        ins.then_inc(act_took, 1)
                    if t == (48, 60)[b]:
                        k = 8 + 4 * b
                        take_hi(ph.turn(0, IN_TURN[f"mix{b}"]), [m0_hi[:, k:k + 4, :].rearrange("p k t -> p (k t)")], [turn[:, :]])
                for n in range(BLOCKS):
                    s, g, T = block_start(n), n // 2, n % 2
                    W = P * (T + 1)
                    if t == s + 2:
                        act.wait_ge(top_ready, n + 1)
                        for j in range(A_PER):
                            a = att[:, n % 2, j * W:(j + 1) * W]
                            nc.scalar.activation(a, a, ACTF.Exp, bias=neg_top[:, j:j + 1], accum_out=sums[:, j:j + 1])
                        nc.scalar.activation(sink_e[:, :], sink_e[:, :], ACTF.Exp).then_inc(exp_done, 1)
                    if t == s + 4:
                        w = CH if T else CH // 2
                        take_hi(ph.turn(0, IN_TURN[f"p{n}"]), [pT[:, 0, 0:w]], [turn[:, 0:w]])
                    if t == s + 5:
                        o4 = turn[:, 0:CH].rearrange("p (k o t) -> p k o t", k=2, o=2)
                        take_hi(ph.turn(0, IN_TURN[f"o{n}"]),
                                [m0_hi[o * 64:o * 64 + 64, 2 * g:2 * g + 2, T * P:(T + 1) * P] for o in range(2)],
                                [o4[o * 64:o * 64 + 64, :, o, :] for o in range(2)])

            def up_work(ph, i, t):
                if t == 9:
                    act.wait_ge(acc_read, 2 * ph.chunk(i, 0) + 2)
                    nc.scalar.activation(hid[:, :, :], hid[:, :, :], ACTF.Silu).then_inc(silu_done, 1)
                if t == ph.slots + 1:
                    take_hi(ph.turn(i), [hT_hi[:, bass.ds(4 * i, 4), :]], [turn[:, :].rearrange("p (k t) -> p k t", k=4)])

            def qkv_work(ph, g, t):
                if t == 9:
                    take_hi(ph.turn(g, 0), [qT1[:, 0:2, :].rearrange("p h t -> p (h t)")], [turn[:, 0:CH]])
                if t == 17:
                    take_hi(ph.turn(g, 1), [kT1[:, 0:2, :].rearrange("p h t -> p (h t)")], [turn[:, 0:CH]])
                zv = zb[:, :].rearrange("p (h c) -> p h c", h=2)[:, :, 0:3 * P]
                for p in range(2):
                    n = 2 * g + p
                    if t == 18 + p:
                        act.wait_ge(z_done, n + 1)
                        nc.scalar.activation(zs[:, p], zv, ACTF.Copy).then_inc(z_copied, 1)
                    if t == 19 + 2 * p:
                        act.wait_ge(z_copied, n + 1)
                        nc.scalar.activation(work[:, p], zs[:, p], ACTF.Abs).then_inc(z_abs, 1)
                    if t == 20 + p:
                        act.wait_ge(z_abs, n + 1)
                        nc.scalar.activation(work[:, p], work[:, p], ACTF.Exp, scale=-1.0).then_inc(z_exp, 1)
                    if t == 20 + 2 * p:
                        act.wait_ge(z_exp, n + 1)
                        nc.scalar.activation(work[:, p], work[:, p], ACTF.Ln, bias=1.0).then_inc(z_log, 1)
                    if t == 23 + 2 * p:
                        act.wait_ge(diff_ready, n + 1)
                        nc.scalar.activation(work[:, p], work[:, p], ACTF.Exp).then_inc(w_exp, 1)
                    if t == 25 + 2 * p:
                        take_hi(ph.turn(g, 2 + p), [m1_hi[:, bass.ds(4 * g + 2 * p, 2), :]],
                                [turn[:, 0:CH].rearrange("p (h t) -> p h t", h=2)])

            def between(ph, i, t):
                if ph.name == "in":
                    in_work(t)
                elif ph.name == "up":
                    up_work(ph, i, t)
                elif ph.name == "qkv":
                    qkv_work(ph, i, t)
                else:
                    residual(ph, i, t)

            act.wait_ge(small_landed, 16 * len(SMALL))
            for n, ph in enumerate(PH):
                def iteration(i, first):
                    for s in range(ph.slots):
                        half(ph, i, s)
                        for work_of in tails(n, i, first, s, 2):
                            between(*work_of)

                iteration(0, True)
                if ph.count > 1:
                    with act.Fori(1, ph.count) as i:
                        iteration(i, False)

        @block.vector
        def _(dve):
            links = [0]

            def link(ins):
                links[0] += 1
                ins.then_inc(dve_chain, 1)
                dve.wait_ge(dve_chain, links[0])

            def half(ph, i, s):
                if ph is PH[0] and s < 8 and s % 2 == 0:
                    q = s // 2
                    dve.wait_ge(xt_hi, q + 1)
                    for k in range(4 * q, 4 * q + 4):
                        ins = nc.vector.scalar_tensor_tensor(out=xT_lo[:, k, :], in0=xT_raw[:, k, :], scalar=normw_sb[:, 0, k:k + 1],
                                                             in1=f32(xT_hi[:, k, :]), op0=ALU.mult, op1=ALU.subtract)
                    ins.then_inc(xt_lo, 1)
                _, nk = ph.tiles(s)
                k = (s % 2) * nk
                dve.wait_ge(hi_ready, ph.half(i, s) + 1)
                nc.vector.tensor_tensor(w_lo[:, s % RING, 0:nk, :], raw[:, (s // 2) % RING, k:k + nk, :],
                                        f32(w_hi[:, s % RING, 0:nk, :]), ALU.subtract).then_inc(lo_ready, 1)

            def evacuate(ph, i, c, dst, const=None):
                for tt in range(TT):
                    dve.wait_ge(products_done, 2 * ph.last_half(i, c) + tt + 1)
                    if const is None:
                        ins = nc.vector.tensor_scalar(dst[:, tt, :], acc[:, acc_pair(ph, c), tt, :], rstd[:, tt:tt + 1], None, ALU.mult)
                    else:
                        ins = nc.vector.tensor_scalar(dst[:, tt, :], acc[:, acc_pair(ph, c), tt, :], rstd[:, tt:tt + 1], const,
                                                      ALU.mult, ALU.mult)
                    ins.then_inc(acc_read, 1)

            def give_var(name, sums_in, width):
                n = roots_per(name)
                if sums_in is not None:
                    shape = sums_in.shape
                    dst = var[:, 0:n]
                    if len(shape) == 4:
                        dst = dst.rearrange("p (t h) -> p t h", t=shape[1])
                    link(nc.vector.tensor_reduce(dst, sums_in, AX.X, ALU.add))
                nc.vector.tensor_scalar(var[:, 0:n], var[:, 0:n], 1.0 / width, EPS, ALU.mult, ALU.add).then_inc(root_var, 1)

            def refine(name, dst=None):
                n = roots_per(name)
                y, v, w = root[:, 0:n], var[:, 0:n], step[:, 0:n]
                dve.wait_ge(root_y, ROOT[name] + 1)
                link(nc.vector.tensor_tensor(w, v, y, ALU.mult))
                link(nc.vector.tensor_tensor(w, w, y, ALU.mult))
                link(nc.vector.tensor_scalar(w, w, -0.5, 1.5, ALU.mult, ALU.add))
                link(nc.vector.tensor_tensor(y if dst is None else dst, y, w, ALU.mult))

            def take_lo(K, dst, src, hi, scale=None):
                dve.wait_ge(act_took, K + 1)
                for n, (d, s, h) in enumerate(zip(dst, src, hi)):
                    if scale is None:
                        ins = nc.vector.tensor_tensor(d, s, f32(h), ALU.subtract)
                    else:
                        ins = nc.vector.scalar_tensor_tensor(out=d, in0=s, scalar=scale[n], in1=f32(h), op0=ALU.mult, op1=ALU.subtract)
                ins.then_inc(dve_took, 1)

            def take(K, dst, src, scale=None):
                dve.wait_ge(turned, K + 1)
                if scale is None:
                    nc.vector.tensor_copy(dst, src).then_inc(dve_took, 1)
                else:
                    nc.vector.tensor_scalar(dst, src, scale, None, ALU.mult).then_inc(dve_took, 1)

            def residual(ph, i, t):
                before, row, name = RESIDUAL[PH.index(ph)]
                if t == ph.slots:
                    if before:
                        dve.wait_ge(kept, 4 * before + (i if row is not None else 0))
                    elif not (isinstance(i, int) and i == 0):
                        dve.wait_ge(kept, i)
                    for tt in range(TT):
                        dve.wait_ge(products_done, 2 * ph.last_half(i, 0) + tt + 1)
                        xs = x_sb[:, tt, bass.ds(i * CH, CH)]
                        dst = xs if row is None else fresh(ph)[:, tt, :]
                        nc.vector.tensor_tensor(dst, acc[:, 0, tt, :], xs, ALU.add).then_inc(x_added, 1)
                if row is None:
                    return
                if t == ph.slots + 1:
                    take_lo(ph.turn(i), [xT_lo[:, bass.ds(i * 4 + k, 1), :] for k in range(4)],
                            [turn[:, k * SEQ:(k + 1) * SEQ] for k in range(4)],
                            [xT_hi[:, bass.ds(i * 4 + k, 1), :] for k in range(4)],
                            [normw_sb[:, row, bass.ds(i * 4 + k, 1)] for k in range(4)])
                if isinstance(i, int) and i == ph.count - 1:
                    if t == ph.slots + 2:
                        dve.wait_ge(squared, TT + 2 * (before + 1) * (D // CH))
                        give_var(name, squares[:, :, :], D)
                    if t == ph.slots + 3:
                        refine(name, rstd[:, :])

            def in_work(t):
                ph = PH[0]
                if t == 4:
                    dve.wait_ge(squared, TT)
                    give_var("x", squares[:, :, 0:1], D)
                if t == 5:
                    refine("x", rstd[:, :])
                if t == 8:
                    evacuate(ph, 0, 0, kv)
                if t == 9:
                    dve.wait_ge(a_squared, 1)
                    give_var("k", sq[:, :, 0:A_KVW].rearrange("p t (h d) -> p t h d", h=A_KV), A_DIM)
                if t == 10:
                    refine("k")
                if t == 11:
                    for tt in range(TT):
                        for o in range(2):
                            ins = nc.vector.tensor_tensor(
                                k2[:, tt, :, o, :], kv[:, tt, 0:A_KVW].rearrange("p (h d) -> p h d", h=A_KV),
                                root[:, tt * A_KV:(tt + 1) * A_KV].unsqueeze(2).to_broadcast([P, A_KV, A_DIM]), ALU.mult)
                    ins.then_inc(k_ready, 1)
                if t == 12:
                    take(ph.turn(0, IN_TURN["k"]), kT[:, 2:4, :].rearrange("p h t -> p (h t)"), turn[:, CH:2 * CH], qkw_sb[:, 1:2])
                for b in range(2):
                    o = 8 * b
                    if t == 16 + o:
                        dve.wait_ge(v_ready, 1)
                        evacuate(ph, 0, 1 + b, qs)
                    if t == 18 + o:
                        dve.wait_ge(a_squared, 2 + b)
                        give_var(f"q{b}", sq[:, :, :].rearrange("p t (h d) -> p (t h) d", d=A_DIM), A_DIM)
                    if t == 19 + o:
                        refine(f"q{b}")
                    if t == 20 + o:
                        q = qs[:, :, :].rearrange("p t (h d) -> p (t h) d", d=A_DIM)
                        nc.vector.tensor_tensor(q, q, root[:, 0:16].unsqueeze(2).to_broadcast([P, 16, A_DIM]),
                                                ALU.mult).then_inc(q_ready, 1)
                    if t == 21 + o:
                        take(ph.turn(0, IN_TURN[f"q{b}"]), qT[:, 4 * b + 2:4 * b + 4, :].rearrange("p h t -> p (h t)"),
                             turn[:, CH:2 * CH], qkw_sb[:, 2:3])
                for b in range(2):
                    o = 16 * b
                    if t == 32 + o:
                        evacuate(ph, 0, 3 + 2 * b, gs)
                    if t == 35 + o:
                        dve.wait_ge(a_squared, 4 + b)
                        give_var(f"g{b}", sq[:, :, :].rearrange("p t (h d) -> p (t h) d", d=B_DIM), B_DIM)
                    if t == 36 + o:
                        refine(f"g{b}")
                    if t in (36 + o, 37 + o):
                        tt = t - 36 - o
                        for g in range(GRP):
                            v = gs[:, tt, g * P:(g + 1) * P]
                            ins = nc.vector.scalar_tensor_tensor(out=v, in0=v, scalar=root[:, tt * GRP + g:tt * GRP + g + 1],
                                                                 in1=gnw_sb[:, (GRP * b + g) * P:(GRP * b + g + 1) * P],
                                                                 op0=ALU.mult, op1=ALU.mult)
                        if tt:
                            ins.then_inc(g_ready, 1)
                    if t == 40 + o:
                        evacuate(ph, 0, 4 + 2 * b, us)
                    if t == (44, 58)[b]:
                        dve.wait_ge(u_gelu, b + 1)
                        dve.wait_ge(turned, ph.turn(0, IN_TURN[f"gate{b}"]) + 1)
                        for g in range(GRP):
                            v = us[:, 0, g * P:(g + 1) * P]
                            ins = nc.vector.scalar_tensor_tensor(out=v, in0=turn[:, g * P:(g + 1) * P],
                                                                 scalar=bs_sb[:, GRP * b + g:GRP * b + g + 1], in1=v,
                                                                 op0=ALU.add, op1=ALU.mult)
                        ins.then_inc(dve_took, 1)
                    if t == (45, 59)[b]:
                        dve.wait_ge(act_took, ph.turn(0, IN_TURN[f"gate{b}"]) + 1)
                        nc.vector.tensor_tensor(us[:, 1, :], us[:, 1, :], sq[:, 1, :], ALU.mult).then_inc(mix_ready, 1)
                    if t == (48, 60)[b]:
                        k = 8 + 4 * b
                        take_lo(ph.turn(0, IN_TURN[f"mix{b}"]), [m0_lo[:, k:k + 4, :].rearrange("p k t -> p (k t)")],
                                [turn[:, :]], [m0_hi[:, k:k + 4, :].rearrange("p k t -> p (k t)")])
                for n in range(BLOCKS):
                    s, g, T = block_start(n), n // 2, n % 2
                    W = P * (T + 1)
                    a = att[:, n % 2, 0:A_PER * W].rearrange("p (j k) -> p j k", j=A_PER)
                    if t == s:
                        dve.wait_ge(logits_done, n + 1)
                        for j in range(A_PER):
                            at = (j % 2) * CH + (j // 2) * W
                            ins = nc.vector.scalar_tensor_tensor(out=a[:, j, :], in0=dist_sb[:, T * P:T * P + W],
                                                                 scalar=SLOPES[A_PER * g + j], in1=zb[:, at:at + W],
                                                                 op0=ALU.mult, op1=ALU.add)
                        ins.then_inc(logits_read, 1)
                    if t == s + 1:
                        sk = sinks_sb[:, A_PER * g:A_PER * (g + 1)]
                        dve.wait_ge(logits_read, n + 1)
                        link(nc.vector.tensor_reduce(top[:, :], a, AX.X, ALU.max))
                        link(nc.vector.tensor_tensor(top[:, :], top[:, :], sk, ALU.max))
                        nc.vector.tensor_tensor(sink_e[:, :], sk, top[:, :], ALU.subtract)
                        nc.vector.tensor_scalar(neg_top[:, :], top[:, :], -1.0, None, ALU.mult).then_inc(top_ready, 1)
                    if t == s + 3:
                        dve.wait_ge(exp_done, n + 1)
                        link(nc.vector.tensor_tensor(sums[:, :], sums[:, :], sink_e[:, :], ALU.add))
                        link(nc.vector.reciprocal(inv[:, :], sums[:, :]))
                        nc.vector.tensor_tensor(a, a, inv[:, :].unsqueeze(2).to_broadcast([P, A_PER, W]), ALU.mult).then_inc(p_ready, 1)
                    if t == s + 4:
                        if T:
                            take(ph.turn(0, IN_TURN[f"p{n}"]), pT[:, 1, :], turn[:, CH:2 * CH])
                        else:
                            take(ph.turn(0, IN_TURN[f"p{n}"]), pT[:, 0, CH // 2:CH], turn[:, CH:CH + CH // 2])
                    if t == s + 5:
                        o4 = turn[:, 0:CH].rearrange("p (k o t) -> p k o t", k=2, o=2)
                        at = [(slice(o * 64, o * 64 + 64), slice(2 * g, 2 * g + 2), slice(T * P, (T + 1) * P)) for o in range(2)]
                        take_lo(ph.turn(0, IN_TURN[f"o{n}"]), [m0_lo[w] for w in at],
                                [o4[o * 64:o * 64 + 64, :, o, :] for o in range(2)], [m0_hi[w] for w in at])

            def up_work(ph, i, t):
                if t == 8:
                    evacuate(ph, i, 0, hid)
                if t == 16:
                    dve.wait_ge(silu_done, ph.layer * ph.count + i + 1)
                    for tt in range(TT):
                        dve.wait_ge(products_done, 2 * ph.last_half(i, 1) + tt + 1)
                        nc.vector.scalar_tensor_tensor(out=hid[:, tt, :], in0=acc[:, 1, tt, :], scalar=rstd[:, tt:tt + 1],
                                                       in1=hid[:, tt, :], op0=ALU.mult, op1=ALU.mult).then_inc(acc_read, 1)
                if t == 17:
                    hv = hT_hi[:, bass.ds(4 * i, 4), :]
                    take_lo(ph.turn(i), [hT_lo[:, bass.ds(4 * i, 4), :]], [turn[:, :].rearrange("p (k t) -> p k t", k=4)], [hv])

            def qkv_work(ph, g, t):
                if t == 8:
                    evacuate(ph, g, 0, qk1, C_DIM ** -0.5)
                if t == 9:
                    take(ph.turn(g, 0), qT1[:, 2:4, :].rearrange("p h t -> p (h t)"), turn[:, CH:2 * CH])
                if t == 16:
                    evacuate(ph, g, 1, qk1)
                if t == 17:
                    take(ph.turn(g, 1), kT1[:, 2:4, :].rearrange("p h t -> p (h t)"), turn[:, CH:2 * CH])
                if t == 24:
                    evacuate(ph, g, 2, v1)
                zv = zb[:, :].rearrange("p (h c) -> p h c", h=2)[:, :, 0:3 * P]
                for p in range(2):
                    n = 2 * g + p
                    if t == 21 + 2 * p:
                        dve.wait_ge(z_log, n + 1)
                        nc.vector.scalar_tensor_tensor(out=soft[:, p], in0=zs[:, p], scalar=0.0, in1=work[:, p],
                                                       op0=ALU.max, op1=ALU.add).then_inc(soft_made, 1)
                        dve.wait_ge(soft_made, n + 1)
                        for h in range(2):
                            d = diagonal(soft[:, p, h])
                            ins = nc.vector.tensor_tensor(d, d, strict_sb[:, :].unsqueeze(1).to_broadcast([P, 2, P]), ALU.mult)
                        ins.then_inc(soft_ready, 1)
                    if t == 22 + 2 * p:
                        dve.wait_ge(sum_done, n + 1)
                        nc.vector.tensor_tensor(work[:, p], zs[:, p], zv, ALU.subtract).then_inc(diff_ready, 1)
                    if t == 24 + 2 * p:
                        dve.wait_ge(w_exp, n + 1)
                        for h in range(2):
                            d = diagonal(work[:, p, h])
                            ins = nc.vector.scalar_tensor_tensor(out=d, in0=d, scalar=1.0,
                                                                 in1=strict_sb[:, :].unsqueeze(1).to_broadcast([P, 2, P]),
                                                                 op0=ALU.min, op1=ALU.mult)
                        ins.then_inc(w_ready, 1)
                    if t == 25 + 2 * p:
                        at = (slice(None), bass.ds(4 * g + 2 * p, 2), slice(None))
                        take_lo(ph.turn(g, 2 + p), [m1_lo[at]], [turn[:, 0:CH].rearrange("p (h t) -> p h t", h=2)], [m1_hi[at]])

            def between(ph, i, t):
                if ph.name == "in":
                    in_work(t)
                elif ph.name == "up":
                    up_work(ph, i, t)
                elif ph.name == "qkv":
                    qkv_work(ph, i, t)
                else:
                    residual(ph, i, t)

            dve.wait_ge(small_landed, 16 * len(SMALL))
            nc.vector.tensor_scalar(qkw_sb[:, 2:3], qkw_sb[:, 0:1], A_DIM ** -0.5, None, ALU.mult).then_inc(scale_ready, 1)
            for n, ph in enumerate(PH):
                def iteration(i, first):
                    for s in range(ph.slots):
                        half(ph, i, s)
                        for work_of in tails(n, i, first, s, 2):
                            between(*work_of)

                iteration(0, True)
                if ph.count > 1:
                    with dve.Fori(1, ph.count) as i:
                        iteration(i, False)
            between(PH[-1], PH[-1].count - 1, PH[-1].slots)

        @block.tensor
        def _(pe):
            def stationary_ready(n, s):
                ph = PH[n]
                if n == 0:
                    pe.wait_ge(xt_lo, s // 2 + 1)
                    return
                prev = PH[n - 1]
                k0, nk = ph.tiles(s)
                if n == 1:
                    K = prev.turn(0, IN_TURN[f"o{2 * s + 1}" if s < 4 else f"mix{(s - 4) // 2}"])
                elif n == 5:
                    K = prev.turn(s // 2, 2 + s % 2)
                else:
                    K = prev.turn((k0 + nk - 1) // 4)
                pe.wait_ge(dve_took, K + 1)

            def accumulator_free(n, i, c, tt, first):
                ph = PH[n]
                if ph.name == "in":
                    if c >= 2:
                        pe.wait_ge(acc_read, 2 * ph.chunk(0, c - 2) + tt + 1)
                elif ph.name in ("out", "down"):
                    if first:
                        i0, c0 = {1: (0, 6), 3: (PH[2].count - 1, 0), 5: (PH[4].count - 1, 2), 7: (PH[6].count - 1, 0)}[n]
                        pe.wait_ge(acc_read, 2 * PH[n - 1].chunk(i0, c0) + tt + 1)
                    else:
                        pe.wait_ge(x_added, 2 * (RESIDUAL[n][0] * (D // CH) + i - 1) + tt + 1)
                elif first and c == 0:
                    pe.wait_ge(x_added, 2 * ((RESIDUAL[n - 1][0] + 1) * (D // CH) - 1) + tt + 1)
                elif c == 2:
                    pe.wait_ge(acc_read, 2 * ph.chunk(i, 0) + tt + 1)
                elif not first:
                    pe.wait_ge(acc_read, 2 * ph.chunk(i - 1, 2 if ph.chunks == 3 and c == 0 else c) + tt + 1)

            def half(n, i, s, first):
                ph = PH[n]
                c, q = s // ph.per_chunk, s % ph.per_chunk
                k0, nk = ph.tiles(s)
                hi, lo = lhs(ph)
                if first and c == 0:
                    stationary_ready(n, s)
                pe.wait_ge(lo_ready, ph.half(i, s) + 1)
                for tt in range(TT):
                    if q == 0:
                        accumulator_free(n, i, c, tt, first)
                    dst = acc[:, acc_pair(ph, c), tt, :]
                    for k in range(nk):
                        h, l = hi[:, k0 + k, tt * P:(tt + 1) * P], lo[:, k0 + k, tt * P:(tt + 1) * P]
                        wh, wl = w_hi[:, s % RING, k, :], w_lo[:, s % RING, k, :]
                        nc.tensor.matmul(dst, h, wh, start=q == 0 and k == 0, stop=False)
                        nc.tensor.matmul(dst, h, wl, start=False, stop=False)
                        ins = nc.tensor.matmul(dst, l, wh, start=False, stop=q == ph.per_chunk - 1 and k == nk - 1)
                    ins.then_inc(products_done, 1)

            def turn_free(K):
                if isinstance(K, int) and K == 0:
                    return
                pe.wait_ge(act_took, K)
                pe.wait_ge(dve_took, K)

            def turn_tiles(K, tiles):
                turn_free(K)
                for at, src in tiles:
                    ins = nc.tensor.transpose(turn[:, at:at + P], src, ident_sb[:, :])
                ins.then_inc(turned, 1)

            def turn_chunk(K, src):
                turn_tiles(K, [(k * SEQ + tt * P, src[:, tt, k * P:(k + 1) * P]) for k in range(4) for tt in range(TT)])

            def residual(ph, i, t):
                before, row, _ = RESIDUAL[PH.index(ph)]
                if row is not None and t == ph.slots + 1:
                    pe.wait_ge(x_added, 2 * (before * (D // CH) + i) + 2)
                    turn_chunk(ph.turn(i), fresh(ph))

            def in_work(t):
                ph = PH[0]
                if t == 12:
                    pe.wait_ge(small_landed, 16 * len(SMALL))
                    pe.wait_ge(cleared, 2)
                    pe.wait_ge(k_ready, 1)
                    turn_tiles(ph.turn(0, IN_TURN["k"]),
                               [(h * SEQ + tt * P, k2[:, tt, h].rearrange("p o d -> p (o d)")) for h in range(A_KV) for tt in range(TT)])
                for b in range(2):
                    if t == 21 + 8 * b:
                        pe.wait_ge(q_ready, b + 1)
                        turn_chunk(ph.turn(0, IN_TURN[f"q{b}"]), qs)
                    if t == (44, 56)[b]:
                        pe.wait_ge(g_ready, b + 1)
                        turn_free(ph.turn(0, IN_TURN[f"gate{b}"]))
                        for tt in range(TT):
                            for g in range(GRP):
                                ins = nc.tensor.matmul(turn[:, tt * CH + g * P:tt * CH + (g + 1) * P], wsT[:, GRP * b + g, :],
                                                       gs[:, tt, g * P:(g + 1) * P], start=True, stop=True)
                        ins.then_inc(turned, 1)
                    if t == (48, 60)[b]:
                        pe.wait_ge(mix_ready, b + 1)
                        turn_chunk(ph.turn(0, IN_TURN[f"mix{b}"]), us)
                for n in range(BLOCKS):
                    s, g, T = block_start(n), n // 2, n % 2
                    W = P * (T + 1)
                    if t == s:
                        K = ph.turn(0, IN_TURN["q0" if g < 2 else "q1"]) + 1
                        pe.wait_ge(act_took, K)
                        pe.wait_ge(dve_took, K)
                        if n:
                            pe.wait_ge(logits_read, n)
                        for j in range(A_PER):
                            o, at = 64 * (j % 2), (j % 2) * CH + (j // 2) * W
                            ins = nc.tensor.matmul(zb[:, at:at + W], qT[o:o + 64, 2 * g + j // 2, T * P:(T + 1) * P],
                                                   kT[o:o + 64, g, 0:W], start=True, stop=True)
                        ins.then_inc(logits_done, 1)
                    if t == s + 4:
                        pe.wait_ge(p_ready, n + 1)
                        a = att[:, n % 2, :]
                        if T:
                            tiles = [(k * CH + j * P, a[:, j * W + k * P:j * W + (k + 1) * P]) for k in range(2) for j in range(A_PER)]
                        else:
                            tiles = [((j // 2) * CH + (j % 2) * P, a[:, j * W:(j + 1) * W]) for j in range(A_PER)]
                        turn_tiles(ph.turn(0, IN_TURN[f"p{n}"]), tiles)
                    if t == s + 5:
                        pe.wait_ge(v_ready, 1)
                        turn_free(ph.turn(0, IN_TURN[f"o{n}"]))
                        for k in range(T + 1):
                            ins = nc.tensor.matmul(turn[:, 0:CH], v2[:, k, g].rearrange("p o d -> p (o d)"), pT[:, k, :],
                                                   start=k == 0, stop=k == T)
                        ins.then_inc(turned, 1)

            def up_work(ph, i, t):
                if t == ph.slots + 1:
                    pe.wait_ge(acc_read, 2 * ph.chunk(i, 1) + 2)
                    turn_chunk(ph.turn(i), hid)

            def qkv_work(ph, g, t):
                if t in (9, 17):
                    c = (t - 9) // 8
                    pe.wait_ge(acc_read, 2 * ph.chunk(g, c) + 2)
                    turn_chunk(ph.turn(g, c), qk1)
                for p in range(2):
                    n = 2 * g + p
                    if t == 18 + p:
                        pe.wait_ge(act_took, ph.turn(g, 1) + 1)
                        pe.wait_ge(dve_took, ph.turn(g, 1) + 1)
                        if p:
                            pe.wait_ge(z_copied, n)
                        elif not (isinstance(g, int) and g == 0):
                            pe.wait_ge(diff_ready, n)
                        for h in range(2):
                            kh, qh = kT1[:, 2 * p + h, :], qT1[:, 2 * p + h, :]
                            nc.tensor.matmul(zb[:, h * CH:h * CH + SEQ], kh[:, 0:P], qh[:, :], start=True, stop=True)
                            ins = nc.tensor.matmul(zb[:, h * CH + SEQ:h * CH + SEQ + P], kh[:, P:], qh[:, P:], start=True, stop=True)
                        ins.then_inc(z_done, 1)
                    if t == 22 + 2 * p:
                        pe.wait_ge(soft_ready, n + 1)
                        if p:
                            pe.wait_ge(diff_ready, n)
                        else:
                            pe.wait_ge(z_copied, n + 2)
                        for h in range(2):
                            z = zb[:, h * CH:h * CH + 3 * P]
                            nc.tensor.matmul(z, tri_sb[:, :], soft[:, p, h, :], start=True, stop=False)
                            ins = nc.tensor.matmul(z[:, P:2 * P], ones_sb[:, :], soft[:, p, h, 2 * P:], start=False, stop=True)
                        ins.then_inc(sum_done, 1)
                    if t == 25 + 2 * p:
                        pe.wait_ge(w_ready, n + 1)
                        pe.wait_ge(acc_read, 2 * ph.chunk(g, 2) + 2)
                        turn_free(ph.turn(g, 2 + p))
                        for h in range(2):
                            col = (2 * p + h) * C_DIM
                            o = turn[:, h * SEQ:(h + 1) * SEQ]
                            nc.tensor.matmul(o, v1[:, 0, col:col + C_DIM], work[:, p, h, 0:2 * P], start=True, stop=False)
                            ins = nc.tensor.matmul(o[:, P:], v1[:, 1, col:col + C_DIM], work[:, p, h, 2 * P:], start=False, stop=True)
                        ins.then_inc(turned, 1)

            def between(ph, i, t):
                if ph.name == "in":
                    in_work(t)
                elif ph.name == "up":
                    up_work(ph, i, t)
                elif ph.name == "qkv":
                    qkv_work(ph, i, t)
                else:
                    residual(ph, i, t)

            for n, ph in enumerate(PH):
                def iteration(i, first):
                    for s in range(ph.slots):
                        for work_of in tails(n, i, first, s, 0):
                            between(*work_of)
                        half(n, i, s, first)

                iteration(0, True)
                if ph.count > 1:
                    with pe.Fori(1, ph.count) as i:
                        iteration(i, False)


def shape_constants():
    r = np.arange(P)
    dist = np.zeros((P, 3 * P), np.float32)
    for tile, cols in ((0, slice(0, P)), (1, slice(P, 3 * P))):
        q = tile * P + r[:, None]
        k = np.arange(P * (tile + 1))[None, :]
        band = (k // CHUNK <= q // CHUNK) & (k // CHUNK > q // CHUNK - 128 // CHUNK)
        dist[:, cols] = np.where(band, -np.abs(q - k), -1e30)
    return {
        "ident": np.eye(P, dtype=np.float32),
        "dist": dist,
        "tri": (r[:, None] >= r[None, :]).astype(np.float32),
        "strict": (r[:, None] < r[None, :]).astype(np.float32),
    }


def kernel(x, mixer_norm_w, ffn_norm_w, w_ffn_gate, w_ffn_up, w_ffn_down, hyb_w_in, hyb_q_norm_w, hyb_k_norm_w,
           hyb_sinks, hyb_gate_norm_w, hyb_w_spatial, hyb_b_spatial, hyb_w_out, sb_w_qkv, sb_w_out):
    from concourse import bacc
    from concourse.bass_utils import run_bass_kernel_spmd

    def lay(a):
        return np.ascontiguousarray(np.asarray(a))

    def feature_major(w):
        return np.asarray(w).reshape(KT, P).T

    x2 = np.asarray(x)[0]
    qw, kw = np.asarray(hyb_q_norm_w)[0], np.asarray(hyb_k_norm_w)[0]
    arrays = {
        "x": lay(x2),
        "xT": lay(x2.T.reshape(KT, P, SEQ).transpose(1, 0, 2)),
        "normw": lay(np.stack([feature_major(w[layer]) for layer in range(2) for w in (mixer_norm_w, ffn_norm_w)], axis=1)),
        "w_gate": lay(w_ffn_gate), "w_up": lay(w_ffn_up), "w_down": lay(w_ffn_down),
        "w_in": lay(hyb_w_in)[0],
        "qkw": lay(np.stack([np.concatenate([qw, qw]), np.concatenate([kw, kw])], axis=1)),
        "sinks": lay(np.broadcast_to(np.asarray(hyb_sinks)[0], (P, A_HEADS))),
        "gnw": lay(np.broadcast_to(np.asarray(hyb_gate_norm_w)[0].reshape(-1), (P, B_W))),
        "ws": lay(np.asarray(hyb_w_spatial)[0].transpose(2, 0, 1)),
        "bs": lay(np.asarray(hyb_b_spatial)[0].T),
        "w_out0": lay(hyb_w_out)[0], "w_qkv": lay(sb_w_qkv)[0], "w_out1": lay(sb_w_out)[0],
        **shape_constants(),
    }
    nc = bacc.Bacc("TRN2", target_bir_lowering=False, num_devices=1)
    aps = {n: nc.dram_tensor(f"in_{n}", a.shape, mybir.dt.from_np(a.dtype), kind="ExternalInput").ap() for n, a in arrays.items()}
    out = nc.dram_tensor("out_0", (SEQ, D), F32, kind="ExternalOutput").ap()
    build(nc, out=out, **aps)
    r = run_bass_kernel_spmd(nc, [{f"in_{n}": a for n, a in arrays.items()}], core_ids=[0])
    return r.results[0]["out_0"].reshape(1, SEQ, D)
```
